# Optimizing a Trainium2 kernel written in Bass

```python
import math
import jax, jax.numpy as jnp
from jax import lax
import numpy as np

D_MODEL = 2048
BATCH = 1
SEQ = 512
DEPTH = 1
DEC_BATCH = 8
DEC_SEQ = 4
PAST_LEN = 4096
PAGE_SIZE = 128

N_MEM = 256
POOL_WIDTH = D_MODEL // 2
CONV_WIDTH = D_MODEL - POOL_WIDTH
POOL_WINDOWS = (2, 4, 8, 16)
N_POOL_GROUPS = len(POOL_WINDOWS)
POOL_GC = POOL_WIDTH // N_POOL_GROUPS
POOL_BUF = max(POOL_WINDOWS) - 1
CONV_K = 3
CONV_BUF = CONV_K - 1
N_CONV_HEADS = 8
IN_COLS = POOL_WIDTH + 3 * CONV_WIDTH
N_XHEADS = 4
XHEAD_DIM = D_MODEL // N_XHEADS
D_FF = 4 * D_MODEL
EPS = 1e-6

kernel_name = "hymba_pool_conv_memxattn_step"

def _rms(x, g):
    xf = x.astype(jnp.float32)
    y = xf * lax.rsqrt(jnp.mean(xf * xf, axis=-1, keepdims=True) + EPS)
    return (y * g.astype(jnp.float32)).astype(x.dtype)

def _pool_mixer(u_prev, u, pos0, w_pool, pool_scale):
    Bn, L, _ = u.shape
    ext = jnp.concatenate([u_prev, u], axis=1).astype(jnp.float32)
    cs = jnp.concatenate([jnp.zeros((Bn, 1, POOL_WIDTH), jnp.float32),
                          jnp.cumsum(ext, axis=1)], axis=1)
    end = cs[:, POOL_BUF + 1:POOL_BUF + 1 + L]
    pos = pos0 + jnp.arange(L)
    outs = []
    for g, w in enumerate(POOL_WINDOWS):
        sl = slice(g * POOL_GC, (g + 1) * POOL_GC)
        start = cs[:, POOL_BUF + 1 - w:POOL_BUF + 1 - w + L, sl]
        count = jnp.minimum(w, pos + 1).astype(jnp.float32)[None, :, None]
        mean = (end[..., sl] - start) / count
        d = (mean - u[..., sl].astype(jnp.float32)).astype(u.dtype)
        outs.append(jnp.einsum('blc,cd->bld', d, w_pool[g]))
    y = jnp.concatenate(outs, axis=-1) * pool_scale
    new_prev = jnp.concatenate([u_prev, u], axis=1)[:, -POOL_BUF:]
    return y, new_prev

def _conv_mixer(conv_prev, bg, cg, v, conv_w):
    L = v.shape[1]
    z = cg * v
    ext = jnp.concatenate([conv_prev, z], axis=1)
    c = conv_w[0] * ext[:, 0:L] + conv_w[1] * ext[:, 1:L + 1] + conv_w[2] * ext[:, 2:L + 2]
    return bg * c, ext[:, -CONV_BUF:]

def _mem_kv(mem, g_mem, w_k, w_v):
    m = _rms(mem, g_mem)
    Bn = mem.shape[0]
    k = (m @ w_k).reshape(Bn, N_MEM, N_XHEADS, XHEAD_DIM)
    v = (m @ w_v).reshape(Bn, N_MEM, N_XHEADS, XHEAD_DIM)
    return k, v

def _cross_attn(h, k, v, w_q, w_o):
    Bn, L, _ = h.shape
    q = (h @ w_q).reshape(Bn, L, N_XHEADS, XHEAD_DIM)
    s = jnp.einsum('blhd,bmhd->bhlm', q, k).astype(jnp.float32) / math.sqrt(XHEAD_DIM)
    p = jax.nn.softmax(s, axis=-1).astype(h.dtype)
    o = jnp.einsum('bhlm,bmhd->blhd', p, v).reshape(Bn, L, D_MODEL)
    return o @ w_o

def _layer(x, mem_k, mem_v, pool_prev, conv_prev, pos0,
           norm_mix, w_in, w_pool, pool_scale, conv_w, w_out,
           norm_attn, w_q, w_o, norm_mlp, w_up, w_down):
    h = _rms(x, norm_mix)
    proj = h @ w_in
    u = proj[..., :POOL_WIDTH]
    bg = proj[..., POOL_WIDTH:POOL_WIDTH + CONV_WIDTH]
    cg = proj[..., POOL_WIDTH + CONV_WIDTH:POOL_WIDTH + 2 * CONV_WIDTH]
    v = proj[..., POOL_WIDTH + 2 * CONV_WIDTH:]
    ya, new_pool = _pool_mixer(pool_prev, u, pos0, w_pool, pool_scale)
    yb, new_conv = _conv_mixer(conv_prev, bg, cg, v, conv_w)
    x = x + jnp.concatenate([ya, yb], axis=-1) @ w_out
    x = x + _cross_attn(_rms(x, norm_attn), mem_k, mem_v, w_q, w_o)
    hm = _rms(x, norm_mlp) @ w_up
    x = x + jnp.square(jax.nn.relu(hm)) @ w_down
    return x, new_pool, new_conv

def setup_inputs(seed: int = 0) -> dict:
    key = jax.random.key(seed)
    ks = jax.random.split(key, 24)
    f = jnp.float32
    n = lambda k, shape, s: jax.random.normal(k, shape, f) * s
    return {
        "x_prompt": n(ks[0], (BATCH, SEQ, D_MODEL), 1.0),
        "x_sample": n(ks[1], (DEC_BATCH, DEC_SEQ, D_MODEL), 1.0),
        "mem_prompt": n(ks[2], (BATCH, N_MEM, D_MODEL), 1.0),
        "cache_mem_k": n(ks[3], (DEPTH, DEC_BATCH, N_MEM, N_XHEADS, XHEAD_DIM), 1.0),
        "cache_mem_v": n(ks[4], (DEPTH, DEC_BATCH, N_MEM, N_XHEADS, XHEAD_DIM), 1.0),
        "state_pool": n(ks[5], (DEPTH, DEC_BATCH, POOL_BUF, POOL_WIDTH), 1.0),
        "state_conv": n(ks[6], (DEPTH, DEC_BATCH, CONV_BUF, CONV_WIDTH), 1.0),
        "norm_mix": 1.0 + n(ks[7], (DEPTH, D_MODEL), 0.05),
        "w_in": n(ks[8], (DEPTH, D_MODEL, IN_COLS), D_MODEL ** -0.5),
        "w_pool": n(ks[9], (DEPTH, N_POOL_GROUPS, POOL_GC, POOL_GC), POOL_GC ** -0.5),
        "pool_scale": 1.0 + n(ks[10], (DEPTH, POOL_WIDTH), 0.05),
        "conv_w": n(ks[11], (DEPTH, CONV_K, CONV_WIDTH), CONV_K ** -0.5),
        "w_out": n(ks[12], (DEPTH, D_MODEL, D_MODEL), D_MODEL ** -0.5),
        "norm_attn": 1.0 + n(ks[13], (DEPTH, D_MODEL), 0.05),
        "norm_mem": 1.0 + n(ks[14], (DEPTH, D_MODEL), 0.05),
        "w_q": n(ks[15], (DEPTH, D_MODEL, D_MODEL), D_MODEL ** -0.5),
        "w_k": n(ks[16], (DEPTH, D_MODEL, D_MODEL), D_MODEL ** -0.5),
        "w_v": n(ks[17], (DEPTH, D_MODEL, D_MODEL), D_MODEL ** -0.5),
        "w_o": n(ks[18], (DEPTH, D_MODEL, D_MODEL), D_MODEL ** -0.5),
        "norm_mlp": 1.0 + n(ks[19], (DEPTH, D_MODEL), 0.05),
        "w_up": n(ks[20], (DEPTH, D_MODEL, D_FF), D_MODEL ** -0.5),
        "w_down": n(ks[21], (DEPTH, D_FF, D_MODEL), D_FF ** -0.5),
        "norm_final": 1.0 + n(ks[22], (D_MODEL,), 0.05),
    }

def reference(x_prompt, x_sample, mem_prompt, cache_mem_k, cache_mem_v, state_pool, state_conv,
              norm_mix, w_in, w_pool, pool_scale, conv_w, w_out,
              norm_attn, norm_mem, w_q, w_k, w_v, w_o,
              norm_mlp, w_up, w_down, norm_final):
    xp, xs = x_prompt, x_sample
    pool_p, conv_p, memk_p, memv_p, pool_s, conv_s = [], [], [], [], [], []
    for l in range(DEPTH):
        lw = (norm_mix[l], w_in[l], w_pool[l], pool_scale[l], conv_w[l], w_out[l],
              norm_attn[l], w_q[l], w_o[l], norm_mlp[l], w_up[l], w_down[l])
        mk, mv = _mem_kv(mem_prompt, norm_mem[l], w_k[l], w_v[l])
        zp = jnp.zeros((xp.shape[0], POOL_BUF, POOL_WIDTH), xp.dtype)
        zc = jnp.zeros((xp.shape[0], CONV_BUF, CONV_WIDTH), xp.dtype)
        xp, npool, nconv = _layer(xp, mk, mv, zp, zc, 0, *lw)
        pool_p.append(npool); conv_p.append(nconv); memk_p.append(mk); memv_p.append(mv)
        xs, spool, sconv = _layer(xs, cache_mem_k[l], cache_mem_v[l], state_pool[l], state_conv[l],
                                  PAST_LEN, *lw)
        pool_s.append(spool); conv_s.append(sconv)
    y_prompt = _rms(xp, norm_final)
    y_sample = _rms(xs, norm_final)
    return (y_prompt, y_sample,
            jnp.stack(pool_p), jnp.stack(conv_p), jnp.stack(memk_p), jnp.stack(memv_p),
            jnp.stack(pool_s), jnp.stack(conv_s))


_drawn_inputs = setup_inputs


def setup_inputs(seed=0):
    import zlib

    import numpy as np

    out = dict(_drawn_inputs(seed))
    spreads = {}
    factors = {'norm_attn': 8.0}
    for name, (base, spread) in spreads.items():
        noise = np.random.default_rng([zlib.crc32(name.encode()), seed]).standard_normal(out[name].shape)
        drawn = base * np.exp(spread * noise) if base else spread * noise
        out[name] = __import__('jax').numpy.asarray(drawn.astype(out[name].dtype))
    for name, factor in factors.items():
        out[name] = (out[name] * factor).astype(out[name].dtype)
    return out
```

```python
import concourse.bass as bass
from concourse import mybir
from contextlib import ExitStack, contextmanager

F32 = mybir.dt.float32
F32R = mybir.dt.float32r
ACT = mybir.ActivationFunctionType
ALU = mybir.AluOpType
AX = mybir.AxisListType
ds = bass.ds

P = 128
D = 2048
KT = D // P
SEQ, NB, DEC = 512, 8, 4
SAMPLE = NB * DEC
TOK = SEQ + SAMPLE
HALF = TOK // 2
CH = 8
MEM = 256
HEADS, HT = 4, 4
HD = HT * P
FF_CHUNKS = 8
WINDOWS = (16, 8, 4, 2)
PAD = 16
POOL_LINE = PAD + SEQ + NB * (PAD + DEC)
POOL_KEEP = 15
CPAD = 2
CONV_LINE = CPAD + SEQ + NB * (CPAD + DEC)
EPS = 1e-6
SCALE = float(HD) ** -0.5
RING = 4
UNIT = 1024
MEM_PIECES = ((0, 2), (2, 4), (4, 8), (8, 12), (12, 16))

G_MIX, G_ATTN, G_MEM, G_MLP, G_FINAL = (KT * n for n in range(5))
POOL_SCALE = 5 * KT
CONV_W = POOL_SCALE + CH
ONES = CONV_W + 3 * CH
IDENT = ONES + P
INV = IDENT + P
OWN = INV + PAD
PARAMS = OWN + 2 * SAMPLE

PHASES = [
    ("mem",      0,  0, 16, 0,  0,  0,  8),
    ("k_proj",  32, 16, 16, 0,  0, 16, 16),
    ("v_proj",  32,  0,  0, 0,  0,  0,  0),
    ("pool_in", 16,  8,  8, 8,  8,  0,  0),
    ("pool_map", 2,  8,  8, 0,  0,  0,  0),
    ("pool_out", 16, 16, 0, 0,  0,  0,  0),
    ("conv_in", 48, 24,  8, 8,  8,  0,  0),
    ("conv_out", 16, 16, 16, 0, 0, 16, 16),
    ("q_proj",  32, 16,  0, 0,  0,  0,  0),
    ("attend_0", 0,  0, 10, 0,  8,  0,  0),
    ("o_proj_0", 16, 16, 0, 0,  0,  0,  0),
    ("attend_1", 0,  0, 10, 0,  8,  0,  0),
    ("o_proj_1", 16, 16, 16, 0, 0, 16, 16),
] + [x for c in range(FF_CHUNKS - 1) for x in (
    (f"up_{c}", 16, 8, 8, 8, 8, 0, 0),
    (f"down_{c}", 16, 16, 0, 0, 0, 0, 0))] + [
    (f"up_{FF_CHUNKS - 1}", 16, 8, 8, 8, 8, 0, 0),
    ("final_0", 16, 16,  0, 0,  0,  0, 16),
    ("final_1", 16, 16,  0, 0,  0,  0, 16)]
COUNTS = ("units", "tiles", "rounded", "values", "b", "a", "squares")


def starts():
    at, out = dict.fromkeys(COUNTS, 0), {}
    for name, *adds in PHASES:
        out[name] = dict(at)
        for key, add in zip(COUNTS, adds):
            at[key] += add
    return out, at


START, TOTAL = starts()
UNITS = TOTAL["units"]

GROUPS = 4
SETS = 4
TURNS = 12


def key_set(h, n):
    return (h // 2 * 4 + h % 2) * SETS + n


def value_set(h, n):
    return (h // 2 * 4 + 2 + h % 2) * SETS + n


class Steps:

    def __init__(self, eng, sem):
        self.eng, self.sem, self.base, self.n = eng, sem, 0, 0

    def did(self, ins):
        ins.then_inc(self.sem, 1)
        self.n += 1

    def settle(self):
        self.eng.wait_ge(self.sem, self.base + self.n)

    def then(self, ins):
        self.did(ins)
        self.settle()

    @contextmanager
    def loop(self, first, last, each):
        before = self.base + self.n
        with self.eng.Fori(first, last) as i:
            self.base, self.n = before + (i - first) * each, 0
            yield i
            assert self.n == each, (self.n, each)
        self.base, self.n = before + (last - first) * each, 0


def build(nc, weights, x_t, mem_t, params, cache_k, cache_v, pool_state, conv_state,
          y_t, k_t, v_out, pool_new, conv_new):
    ctx = ExitStack()
    with ctx:
        place = [(nc.sbuf_base + 31) // 32 * 32]

        def at(name, shape, dtype, offset):
            return nc.alloc_sbuf_tensor_at(name, shape, dtype, offset=offset)

        def room(n):
            place[0] += (n + 31) // 32 * 32
            return place[0] - (n + 31) // 32 * 32

        a_at = room(KT * 2 * TOK * 4)
        b_at = room(CH * 2 * TOK * 4)
        A = at("inner_a", [P, KT, 2, TOK], F32R, a_at)
        B = at("inner_b", [P, CH, 2, TOK], F32R, b_at)
        MEMS = at("mem_split", [P, KT, 2, MEM], F32R, b_at)
        Q = at("queries", [P, KT, TOK], F32, b_at)
        a_half = a_at + CH * 2 * TOK * 4
        MEM_RAW = at("mem_raw", [P, KT, MEM], F32, a_half)
        Y = at("y_out", [P, KT, TOK], F32, a_at)
        X = at("residual", [P, KT, TOK], F32, room(KT * TOK * 4))
        RAW = at("unit_raw", [P, RING, UNIT], F32, room(RING * UNIT * 4))
        WHI = at("unit_high", [P, RING, UNIT], F32R, room(RING * UNIT * 4))
        WLO = at("unit_low", [P, RING, UNIT], F32R, room(RING * UNIT * 4))
        PAR = at("par", [P, PARAMS], F32, room(PARAMS * 4))
        RSTD = at("rstd", [P, TOK], F32, room(TOK * 4))
        SUMS = at("square_sums", [P, TOK], F32, room(TOK * 4))
        RSTDM = at("rstd_mem", [P, MEM + 2], F32, room((MEM + 2) * 4))
        t_at = room(5 * POOL_LINE * 4)
        TA, TB, TC, TD, TE = (at(f"temp_{n}", [P, POOL_LINE], F32, t_at + n * POOL_LINE * 4) for n in range(5))
        PSTATE = at("pool_state_in", [P, 2, NB * PAD], F32, room(2 * NB * PAD * 4))
        PNEW = at("pool_new_out", [P, 2, (NB + 1) * POOL_KEEP], F32, room(2 * (NB + 1) * POOL_KEEP * 4))
        CSTATE = at("conv_state_in", [P, CH, NB * CPAD], F32, room(CH * NB * CPAD * 4))
        cnew_at = room(CH * (NB + 1) * CPAD * 4)
        CNEW = at("conv_new_out", [P, CH, (NB + 1) * CPAD], F32, cnew_at)
        ROWMAX, NEGMAX, ROWSUM, ROWINV = (
            at(name, [P, 12], F32, room(48)) for name in ("row_max", "row_negmax", "row_sum", "row_inv"))
        assert place[0] <= nc.sbuf_usable_end, place[0]
        KV = at("kv_heads", [P, 2, UNIT], F32, a_half)
        CACHE_A = at("cache_ring_a", [P, 2, GROUPS, 512], F32, a_half + 8192)
        PT = at("probs_turned", [P, 2, SEQ], F32, a_half + 24576)
        PS = at("sample_probs_turned", [P, 2, 2, P], F32, a_half + 28672)
        OS = at("sample_out", [P, 2, HD], F32, a_half + 30720)
        CACHE_T = at("cache_ring_t", [P, 2, GROUPS, 512], F32, t_at)
        PROBS = at("probs", [P, 12, MEM], F32, t_at)
        KEYS = at("keys_even", [P, UNIT], F32, t_at + 12288)
        assert cnew_at - t_at >= 16384 and CH * 2 * TOK * 4 >= 34816

        M = ctx.enter_context(nc.psum_tensor("psum_main", [P, 4, 512], F32))
        S = ctx.enter_context(nc.psum_tensor("psum_side", [P, 4, 512], F32))

        def sem(name):
            return ctx.enter_context(nc.semaphore(name))

        raw_loaded = [sem(f"raw_loaded_{s}") for s in range(RING)]
        high_ready = sem("high_ready")
        split_ready = sem("split_ready")
        units_used = sem("units_used")
        psum_free = sem("psum_free")
        values = sem("values_made")
        rounded = sem("rounded")
        mem_ready = sem("mem_ready")
        a_ready = sem("a_ready")
        b_ready = sem("b_ready")
        squared = sem("squared")
        summed = sem("summed")
        sums_done = sem("sums_done")
        warm = sem("warm")
        var_ready = sem("var_ready")
        root_ready = sem("root_ready")
        y_ready = sem("y_ready")
        y_stored = [sem(f"y_stored_{n}") for n in range(2)]
        par_loaded = sem("par_loaded")
        mem_loaded = [sem(f"mem_loaded_{n}") for n in range(len(MEM_PIECES))]
        x_loaded = [sem(f"x_loaded_{n}") for n in range(KT // 2)]
        k_stored = [sem(f"k_stored_{n}") for n in range(2)]
        v_stored = [sem(f"v_stored_{n}") for n in range(2)]
        v_staged = sem("v_staged")
        pool_loaded = [sem(f"pool_loaded_{n}") for n in range(2)]
        pool_kept = sem("pool_kept")
        pool_stored = [sem(f"pool_stored_{n}") for n in range(2)]
        group_done = sem("group_done")
        conv_loaded = sem("conv_loaded")
        conv_kept = sem("conv_kept")
        conv_stored = sem("conv_stored")
        keys_loaded = [sem(f"keys_loaded_{n}") for n in range(2)]
        values_loaded = [sem(f"values_loaded_{n}") for n in range(2)]
        cache_loaded = [sem(f"cache_loaded_{n}") for n in range(2)]
        cache_used = sem("cache_used")
        heads_scored = sem("heads_scored")
        negmax_ready = sem("negmax_ready")
        exps = sem("exps")
        probs_ready = sem("probs_ready")
        turned = sem("turned")
        turned_out = sem("turned_out")
        os_copied = sem("os_copied")
        pv_done = sem("pv_done")
        dve_steps = sem("dve_steps")

        block = ctx.enter_context(nc.Block())

        def halves(ap):
            return ap.rearrange("p (a b) -> p a b", a=2)

        def pool_map_out(c):
            return (M, S)[c // 2 % 2][:, 2 * (c % 2):2 * (c % 2) + 2, 0:HALF]

        def turned_at(item):
            return item % 2

        def cache_ring(n):
            return (CACHE_T if n < 2 * SETS else CACHE_A)[:, n % 2]

        def unit(name, extra, n):
            u = START[name]["units"] + n
            return extra + u // RING, u % RING

        def later(u, n):
            return u[0] + (u[1] + n) // RING, (u[1] + n) % RING

        def count(u):
            return u[0] * RING + (u[1] + 1)

        @block.sync
        def _(sp):
            def load(turn, s):
                sp.dma_start(RAW[:, s, :], weights[turn * RING + s]).then_inc(raw_loaded[s], 16)

            mem_v = mem_t.rearrange("(k p) m -> p k m", p=P)
            sp.dma_start(PAR[:, :], params).then_inc(par_loaded, 16)
            for n, (k0, k1) in enumerate(MEM_PIECES):
                sp.dma_start(MEM_RAW[:, k0:k1, :], mem_v[:, k0:k1, :]).then_inc(mem_loaded[n], 16)
                if n != 1:
                    load(0, max(0, n - 1))
            with sp.Fori(1, UNITS // RING) as turn:
                for s in range(RING):
                    sp.wait_ge(split_ready, turn * RING + (s + 1 - RING))
                    load(turn, s)
            for s in range(UNITS % RING):
                sp.wait_ge(split_ready, UNITS - UNITS % RING + s + 1 - RING)
                load(UNITS // RING, s)
            for t in range(0, KT, 2):
                sp.wait_ge(y_ready, KT + t + 2)
                sp.dma_start(y_t[1, :, t:t + 2, :], Y[:, t:t + 2, HALF:TOK]).then_inc(y_stored[1], 16)
            sp.wait_ge(y_stored[1], 16 * KT // 2)

        @block.gpsimd
        def _(pool):
            x_v = x_t.rearrange("(k p) n -> p k n", p=P)
            pool.wait_ge(mem_loaded[len(MEM_PIECES) - 1], 16)

            def load_x(n):
                pool.dma_start(X[:, 2 * n:2 * n + 2, :], x_v[:, 2 * n:2 * n + 2, :]).then_inc(x_loaded[n], 16)

            load_x(0)
            for n in range(1, 3):
                pool.wait_ge(units_used, 2 * n)
                load_x(n)
            pool.dma_start(CSTATE[:, :, :], conv_state).then_inc(conv_loaded, 16)
            for n in range(2):
                pool.dma_start(PSTATE[:, n, :], pool_state[n]).then_inc(pool_loaded[n], 16)

            for i in range(KT // 2):
                for j in range(2):
                    pool.wait_ge(psum_free, i * 2 + (j + 1))
                    pool.dma_start(k_t[i * 2 + j], (TC, TD)[j][:, 0:MEM]).then_inc(k_stored[j], 16)
                if i + 3 < KT // 2:
                    load_x(i + 3)
            with pool.Fori(0, D // 512) as i:
                for j in range(2):
                    pool.wait_ge(v_staged, i * 2 + (j + 1))
                    pool.dma_start(v_out[i, j], (TC, TD)[j][:, 0:512]).then_inc(v_stored[j], 16)

            for c in range(CH):
                pool.wait_ge(pool_kept, c + 1)
                pool.dma_start(pool_new[c], PNEW[:, c % 2, :]).then_inc(pool_stored[c % 2], 16)
                if c + 2 < CH:
                    pool.dma_start(PSTATE[:, c % 2, :], pool_state[c + 2]).then_inc(pool_loaded[c % 2], 16)
            pool.wait_ge(conv_kept, CH)
            pool.dma_start(conv_new, CNEW[:, :, :]).then_inc(conv_stored, 16)

            for j in range(2):
                pool.wait_ge(k_stored[j], 16 * KT // 2)
                pool.wait_ge(v_stored[j], 16 * D // 512)

            def load_set(source, h, n):
                at = (key_set if source is cache_k else value_set)(h, n)
                if at >= 2:
                    pool.wait_ge(cache_used, at - 1)
                pool.dma_start(cache_ring(at), source[SETS * h + n].rearrange("p (j n) -> p j n", j=GROUPS)) \
                    .then_inc(cache_loaded[at % 2], 16)

            def load_keys(h):
                pool.dma_start((KV[:, 1, :] if h % 2 else KEYS[:, :]).rearrange("p (k m) -> p k m", k=HT),
                               k_t[HT * h:HT * h + HT].rearrange("k p m -> p k m")).then_inc(keys_loaded[h % 2], 16)

            def load_values(h):
                pool.dma_start(KV[:, h % 2, :].rearrange("p (t d) -> p t d", t=2),
                               v_out[h].rearrange("t p d -> p t d")).then_inc(values_loaded[h % 2], 16)

            pool.wait_ge(psum_free, START["q_proj"]["tiles"] + 1)
            for n in range(2 * SETS):
                load_set(cache_k, n // SETS, n % SETS)
            pool.wait_ge(cache_used, 2 * SETS)
            load_keys(0)
            pool.wait_ge(psum_free, START["attend_0"]["tiles"])
            load_keys(1)
            for g in range(2):
                h = 2 * g
                load_set(cache_v, h, 0)
                load_set(cache_v, h, 1)
                if g:
                    pool.wait_ge(pv_done, HT * (h - 1))
                load_values(h)
                load_set(cache_v, h, 2)
                load_set(cache_v, h, 3)
                pool.wait_ge(heads_scored, 4 * (h + 2))
                load_values(h + 1)
                for n in range(SETS):
                    load_set(cache_v, h + 1, n)
                if g == 0:
                    load_keys(2)
                    pool.wait_ge(pv_done, 2 * HT)
                    load_keys(3)
                    for n in range(2 * SETS):
                        load_set(cache_k, 2 + n // SETS, n % SETS)
            for t in range(0, KT, 4):
                pool.wait_ge(y_ready, t + 4)
                pool.dma_start(y_t[0, :, t:t + 4, :], Y[:, t:t + 4, 0:HALF]).then_inc(y_stored[0], 16)
            for n in range(2):
                pool.wait_ge(pool_stored[n], 16 * CH // 2)
            pool.wait_ge(conv_stored, 16)
            pool.wait_ge(y_stored[0], 16 * KT // 4)

        @block.scalar
        def _(act):
            def convert(u):
                turn, s = u
                act.wait_ge(raw_loaded[s], turn * 16 + 16)
                act.activation(WHI[:, s, :], RAW[:, s, :], ACT.Copy).then_inc(high_ready, 1)

            def convert_next(u):
                act.wait_ge(units_used, count(u))
                convert(later(u, RING))

            def root(n, source):
                act.wait_ge(var_ready, n + 1)
                act.activation(TC[:, 0:source.shape[1]], source, ACT.Sqrt).then_inc(root_ready, 1)

            def square(k, n, source, width):
                act.wait_ge(summed, n - 1)
                act.activation((TA, TB)[k % 2][:, 0:width], source, ACT.Square).then_inc(squared, 1)

            def round_a(t, gain):
                act.activation(A[:, t, 0, :], X[:, t, :], ACT.Identity, scale=PAR[:, gain + t:gain + t + 1]) \
                    .then_inc(rounded, 1)

            act.wait_ge(dve_steps, 1)
            act.activation(TC[:, 0:1], SUMS[:, 0:1], ACT.Copy).then_inc(warm, 1)

            act.wait_ge(par_loaded, 16)
            for n, (k0, k1) in enumerate(MEM_PIECES):
                act.wait_ge(mem_loaded[n], 16)
                for k in range(k0, k1):
                    act.activation(MEMS[:, k, 0, :], MEM_RAW[:, k, :], ACT.Identity,
                                   scale=PAR[:, G_MEM + k:G_MEM + k + 1]).then_inc(rounded, 1)
                if n in (0, 2, 4):
                    convert((0, n // 2))
            for k in range(CH):
                if k >= 2:
                    act.wait_ge(summed, k - 1)
                act.activation((TA, TB)[k % 2][:, 0:2 * MEM].rearrange("p (a m) -> p a m", a=2),
                               MEM_RAW[:, 2 * k:2 * k + 2, :], ACT.Square).then_inc(squared, 1)
                if k == 1:
                    convert((0, 3))
                elif k % 2 == 1:
                    convert_next(unit("k_proj", 0, k // 2 - 1))
            root(0, RSTDM[:, :])
            convert_next(unit("k_proj", 0, 3))

            for t in range(KT):
                if t % 2 == 0:
                    act.wait_ge(x_loaded[t // 2], 16)
                round_a(t, G_MIX)
                square(t, t + CH, X[:, t, :], TOK)
                if t < KT - 2:
                    for n in (4, 5):
                        convert_next(unit("k_proj", 0, 2 * t + n))

            with act.Fori(0, 8) as i:
                for j in range(4):
                    convert_next(unit("v_proj", i, j))

            root(1, RSTD[:, :])
            s0 = START["pool_in"]
            for c in range(CH):
                for n in range(2):
                    convert_next(unit("pool_in", 0, 2 * c + n))
                act.wait_ge(values, s0["values"] + c + 1)
                act.activation(B[:, c, 0, :], TE[:, 0:TOK], ACT.Copy).then_inc(rounded, 1)

            for g in range(4):
                if g % 2 == 0:
                    act.wait_ge(group_done, g // 2 + 1)
                else:
                    act.wait_ge(units_used, START["pool_map"]["units"] + g // 2 + 1)
                for n in range(2):
                    c = 2 * g + n
                    act.activation(halves(B[:, c, 0, :]), pool_map_out(c), ACT.Identity,
                                   scale=PAR[:, POOL_SCALE + c:POOL_SCALE + c + 1]).then_inc(rounded, 1)
                if g % 2 == 1:
                    convert_next(unit("pool_map", 0, g // 2))

            def down(name, extra=0, groups=4):
                with act.Fori(0, groups) as i:
                    for j in range(4):
                        convert_next(unit(name, i + extra, j))

            def down_last(name, gain):
                s = START[name]
                for i in range(4):
                    for j in range(4):
                        t = i * 4 + j
                        convert_next(unit(name, i, j))
                        act.wait_ge(psum_free, t + (s["tiles"] + 1))
                        round_a(t, gain)
                        square(j, t + s["squares"], X[:, t, :], TOK)

            down("pool_out")
            s0 = START["conv_in"]
            for i in range(CH // 2):
                for j in range(2):
                    for n in range(6):
                        convert_next(unit("conv_in", i * 3, 6 * j + n))
                    act.wait_ge(values, i * 2 + (s0["values"] + j + 1))
                    act.activation(B[:, i * 2 + j, 0, :], TB[:, 0:TOK], ACT.Copy).then_inc(rounded, 1)
            down_last("conv_out", G_ATTN)

            root(2, RSTD[:, :])
            with act.Fori(0, 8) as i:
                for j in range(4):
                    convert_next(unit("q_proj", i, j))

            def attend(g):
                for j in range(2):
                    act.wait_ge(negmax_ready, 10 * g + j + 1)
                    for r in range(2):
                        e = 2 * j + r
                        act.activation(PROBS[:, e, :], S[:, 2 + j, r * MEM:r * MEM + MEM], ACT.Exp,
                                       bias=NEGMAX[:, e:e + 1], scale=SCALE,
                                       accum_out=ROWSUM[:, e:e + 1]).then_inc(exps, 1)
                for p in range(8):
                    act.wait_ge(negmax_ready, 10 * g + p + 3)
                    act.activation(PROBS[:, 4 + p, :], M[:, p % 4, 0:MEM], ACT.Exp, bias=NEGMAX[:, 4 + p:5 + p],
                                   scale=SCALE, accum_out=ROWSUM[:, 4 + p:5 + p]).then_inc(exps, 1)
                tiles = A if g == 0 else B

                def high_prompt(c):
                    act.wait_ge(pv_done, 8 * g + c + 1)
                    act.activation(tiles[:, c, 0, 0:SEQ], M[:, c % 4, 0:SEQ], ACT.Copy).then_inc(rounded, 1)

                def high_samples(j):
                    item = TURNS * g + (6, 11)[j]
                    act.wait_ge(turned, item + 1)
                    act.activation(tiles[:, HT * j:HT * j + HT, 0, SEQ:TOK],
                                   S[:, turned_at(item), 0:P].rearrange("p (c n) -> p c n", c=HT),
                                   ACT.Copy).then_inc(rounded, 1)

                for c in (0, 1, 2):
                    high_prompt(c)
                high_samples(0)
                for c in (3, 4, 5, 6):
                    high_prompt(c)
                high_samples(1)
                high_prompt(7)

            attend(0)
            down("o_proj_0")
            attend(1)
            down_last("o_proj_1", G_MLP)

            root(3, RSTD[:, :])

            def up(c):
                s = START["up_0"]
                for i in range(4):
                    for j in range(2):
                        for n in range(2):
                            convert_next(unit("up_0", i + c * 8, 2 * j + n))
                        act.wait_ge(values, c * 8 + i * 2 + (s["values"] + j + 1))
                        act.activation(B[:, i * 2 + j, 0, :], TB[:, 0:TOK], ACT.Copy).then_inc(rounded, 1)

            with act.Fori(0, FF_CHUNKS - 1) as c:
                up(c)
                down("down_0", c * 8)
            up(FF_CHUNKS - 1)
            for h in range(2):
                s = START[f"final_{h}"]
                half = slice(h * HALF, h * HALF + HALF)
                for t in range(KT):
                    if h == 0 or t < KT - RING:
                        convert_next(unit(f"final_{h}", 0, t))
                    act.wait_ge(psum_free, s["tiles"] + t + 1)
                    square(t, t + s["squares"], X[:, t, half], HALF)
                    if h == 1 and t == 3:
                        root(4, RSTD[:, 0:HALF])
            root(5, RSTD[:, HALF:TOK])

        @block.vector
        def _(dve):
            steps = Steps(dve, dve_steps)

            def convert(u):
                dve.wait_ge(high_ready, count(u))
                s = u[1]
                dve.tensor_tensor(WLO[:, s, :], RAW[:, s, :], WHI[:, s, :].bitcast(F32), ALU.subtract) \
                    .then_inc(split_ready, 1)

            def convert_next(u):
                convert(later(u, RING))

            def add_squares(k, n, out, width):
                dve.wait_ge(squared, n + 1)
                dve.wait_ge(summed, n)
                dve.tensor_tensor(out[:, 0:width], out[:, 0:width], (TA, TB)[k % 2][:, 0:width], ALU.add) \
                    .then_inc(summed, 1)

            def rstd(n, source, out, flat):
                dve.wait_ge(sums_done, n + 1)
                dve.tensor_scalar(out, source, 1.0 / D, EPS, ALU.mult, ALU.add).then_inc(var_ready, 1)
                width = flat.shape[1]
                r, y, z = TC[:, 0:width], TD[:, 0:width], TE[:, 0:width]
                dve.wait_ge(root_ready, n + 1)
                steps.then(dve.reciprocal(y, r))
                steps.then(dve.tensor_tensor(z, y, y, ALU.mult))
                steps.then(dve.scalar_tensor_tensor(z, z, -0.5, flat, ALU.mult, ALU.mult))
                steps.then(dve.scalar_tensor_tensor(flat, z, 1.5, y, ALU.add, ALU.mult))

            def rstd_tokens(n, squares):
                dve.wait_ge(summed, squares)
                dve.wait_ge(sums_done, n + 1)
                steps.did(dve.memset(SUMS[:, :], 0.0))
                rstd(n, S[:, 0:2, 0:HALF], halves(RSTD[:, :]), RSTD[:, :])

            def low_a(t, count_rounded, gain):
                dve.wait_ge(rounded, count_rounded)
                dve.scalar_tensor_tensor(A[:, t, 1, :], X[:, t, :], PAR[:, ds(t + gain, 1)],
                                         A[:, t, 0, :].bitcast(F32), ALU.mult, ALU.subtract).then_inc(a_ready, 1)

            def product(u):
                dve.wait_ge(units_used, count(u))

            steps.did(dve.memset(SUMS[:, :], 0.0))
            steps.then(dve.memset(TE[:, 0:2 * MEM], 0.0))
            dve.wait_ge(par_loaded, 16)
            for n, (k0, k1) in enumerate(MEM_PIECES):
                for k in range(k0, k1):
                    dve.wait_ge(rounded, k + 1)
                    dve.scalar_tensor_tensor(MEMS[:, k, 1, :], MEM_RAW[:, k, :], PAR[:, G_MEM + k:G_MEM + k + 1],
                                             MEMS[:, k, 0, :].bitcast(F32), ALU.mult, ALU.subtract) \
                        .then_inc(mem_ready, 1)
                if n in (0, 2, 4):
                    convert((0, n // 2))
            for k in range(CH):
                dve.wait_ge(squared, k + 1)
                if k:
                    dve.wait_ge(summed, k)
                dve.tensor_tensor(TE[:, 0:2 * MEM], TE[:, 0:2 * MEM], (TA, TB)[k % 2][:, 0:2 * MEM], ALU.add) \
                    .then_inc(summed, 1)
                if k == 1:
                    convert((0, 3))
                elif k % 2 == 1:
                    convert_next(unit("k_proj", 0, k // 2 - 1))
            dve.wait_ge(warm, 1)
            rstd(0, S[:, 0, 0:MEM + 2], RSTDM[:, :], RSTDM[:, :])
            convert_next(unit("k_proj", 0, 3))

            s0 = START["k_proj"]

            def key_tile(i, j, more=True):
                t = i * 4 + j
                if j >= 2 or not isinstance(i, int) or i:
                    dve.wait_ge(k_stored[j % 2], i * 32 + 16 * (j // 2))
                product(unit("k_proj", i * 2, 2 * j + 1))
                dve.tensor_tensor((TC, TD)[j % 2][:, 0:MEM], M[:, j, 0:MEM], RSTDM[:, 0:MEM], ALU.mult) \
                    .then_inc(psum_free, 1)
                low_a(t, t + (s0["rounded"] + 1), G_MIX)
                add_squares(j, t + s0["squares"], SUMS, TOK)
                if more:
                    for n in (4, 5):
                        convert_next(unit("k_proj", i * 2, 2 * j + n))

            for j in range(4):
                key_tile(0, j)
            with dve.Fori(1, 3) as i:
                for j in range(4):
                    key_tile(i, j)
            for j in range(4):
                key_tile(3, j, j < 2)

            for j in range(2):
                dve.wait_ge(k_stored[j], 16 * KT // 2)

            for i in range(4):
                for n in range(8):
                    if n < 7:
                        convert_next(unit("v_proj", 2 * i, n))
                product(unit("v_proj", 2 * i, 7))
                for j in range(2):
                    if i:
                        dve.wait_ge(v_stored[j], 16 * i)
                    dve.tensor_scalar((TC, TD)[j][:, 0:512], M[:, 2 * (i % 2) + j, 0:512],
                                      RSTDM[:, MEM + j:MEM + j + 1], None, ALU.mult).then_inc(v_staged, 1)
                convert_next(unit("v_proj", 2 * i, 7))

            s0 = START["pool_in"]
            for j in range(2):
                dve.wait_ge(v_stored[j], 16 * 4)
            rstd_tokens(1, s0["squares"])
            steps.then(dve.memset(TA[:, :], 0.0))
            line = lambda t: t[:, PAD:PAD + SEQ]
            own = lambda t: t[:, PAD + SEQ:POOL_LINE].rearrange("p (b n) -> p b n", b=NB)
            by_row = lambda ap: ap.rearrange("p (b n) -> p b n", b=NB)
            for c in range(CH):
                w = WINDOWS[c // 2]
                ps = M[:, 2 * (c % 2):2 * (c % 2) + 2, 0:HALF]
                convert_next(unit("pool_in", 0, 2 * c))
                product(unit("pool_in", 0, 2 * c + 1))
                dve.wait_ge(values, c) if c else None
                steps.did(dve.tensor_tensor(TA[:, PAD:PAD + HALF], ps[:, 0, :], RSTD[:, 0:HALF], ALU.mult))
                steps.did(dve.tensor_tensor(TA[:, PAD + HALF:PAD + SEQ], ps[:, 1, 0:SEQ - HALF],
                                            RSTD[:, HALF:SEQ], ALU.mult))
                dve.tensor_tensor(own(TA)[:, :, PAD:PAD + DEC], by_row(ps[:, 1, SEQ - HALF:HALF]),
                                  by_row(RSTD[:, SEQ:TOK]), ALU.mult).then_inc(psum_free, 1)
                dve.wait_ge(pool_loaded[c % 2], 16 * (c // 2 + 1))
                steps.then(dve.tensor_copy(own(TA)[:, :, 0:PAD], by_row(PSTATE[:, c % 2, :])))
                dve.wait_ge(psum_free, s0["tiles"] + c + 1)
                if c >= 2:
                    dve.wait_ge(pool_stored[c % 2], 16 * (c // 2))
                steps.then(dve.tensor_copy(PNEW[:, c % 2, 0:POOL_KEEP], TA[:, PAD + SEQ - POOL_KEEP:PAD + SEQ]))
                dve.tensor_copy(by_row(PNEW[:, c % 2, POOL_KEEP:]), own(TA)[:, :, PAD + DEC - POOL_KEEP:]) \
                    .then_inc(pool_kept, 1)
                total, spare, shift = TA, [TC, TD], 1
                while shift < w:
                    out, lo = spare[0], 2 * shift - 1
                    steps.then(dve.tensor_tensor(out[:, lo:POOL_LINE], total[:, lo:POOL_LINE],
                                                 total[:, lo - shift:POOL_LINE - shift], ALU.add))
                    total, spare, shift = out, spare[::-1], 2 * shift
                if c:
                    dve.wait_ge(b_ready, c)
                steps.then(dve.tensor_tensor(TB[:, 0:w - 1], line(total)[:, 0:w - 1], PAR[:, INV:INV + w - 1],
                                             ALU.mult))
                steps.did(dve.tensor_tensor(TE[:, 0:w - 1], TB[:, 0:w - 1], line(TA)[:, 0:w - 1], ALU.subtract))
                steps.then(dve.scalar_tensor_tensor(TE[:, w - 1:SEQ], line(total)[:, w - 1:], 1.0 / w,
                                                    line(TA)[:, w - 1:], ALU.mult, ALU.subtract))
                dve.scalar_tensor_tensor(by_row(TE[:, SEQ:TOK]), own(total)[:, :, PAD:], 1.0 / w,
                                         own(TA)[:, :, PAD:], ALU.mult, ALU.subtract).then_inc(values, 1)
                convert_next(unit("pool_in", 0, 2 * c + 1))
                dve.wait_ge(rounded, s0["rounded"] + c + 1)
                dve.tensor_tensor(B[:, c, 1, :], TE[:, 0:TOK], B[:, c, 0, :].bitcast(F32), ALU.subtract) \
                    .then_inc(b_ready, 1)

            s0 = START["pool_map"]
            for c in range(CH):
                dve.wait_ge(rounded, s0["rounded"] + c + 1)
                dve.scalar_tensor_tensor(halves(B[:, c, 1, :]), pool_map_out(c),
                                         PAR[:, POOL_SCALE + c:POOL_SCALE + c + 1],
                                         halves(B[:, c, 0, :]).bitcast(F32), ALU.mult, ALU.subtract) \
                    .then_inc(psum_free, 1)
                if c % 4 == 3:
                    convert_next(unit("pool_map", 0, c // 4))

            def add_to_residual(u, t, j):
                product(u)
                dve.tensor_tensor(halves(X[:, t, :]), M[:, 2 * (j % 2):2 * (j % 2) + 2, 0:HALF],
                                  halves(X[:, t, :]), ALU.add).then_inc(psum_free, 1)

            def down(name, extra=0):
                with dve.Fori(0, 4) as i:
                    for j in range(4):
                        u = unit(name, i + extra, j)
                        add_to_residual(u, i * 4 + j, j)
                        convert_next(u)

            def down_last(name, gain):
                s = START[name]
                with dve.Fori(0, 4) as i:
                    for j in range(4):
                        t, u = i * 4 + j, unit(name, i, j)
                        add_to_residual(u, t, j)
                        convert_next(u)
                        low_a(t, t + (s["rounded"] + 1), gain)
                        add_squares(j, t + s["squares"], SUMS, TOK)

            down("pool_out")

            s0 = START["conv_in"]
            line = lambda t, back=0: t[:, CPAD - back:CONV_LINE - back]
            own = lambda t: t[:, CPAD + SEQ:CONV_LINE].rearrange("p (b n) -> p b n", b=NB)
            dve.wait_ge(conv_loaded, 16)
            steps.then(dve.memset(TC[:, 0:CPAD], 0.0))
            with steps.loop(0, CH // 2, 16) as i:
                for j in range(2):
                    c = i * 2 + j

                    def evacuate(n, out):
                        convert_next(unit("conv_in", i * 3, 6 * j + 2 * n))
                        product(unit("conv_in", i * 3, 6 * j + 2 * n + 1))
                        m = 2 * ((3 * j + n) % 2)
                        dve.tensor_tensor(halves(out[:, 0:TOK]), M[:, m:m + 2, 0:HALF], halves(RSTD[:, :]),
                                          ALU.mult).then_inc(psum_free, 1)
                        convert_next(unit("conv_in", i * 3, 6 * j + 2 * n + 1))

                    dve.wait_ge(values, c + s0["values"])
                    dve.wait_ge(b_ready, c + s0["b"])
                    evacuate(0, TA)
                    evacuate(1, TB)
                    dve.wait_ge(psum_free, i * 6 + (s0["tiles"] + 3 * j + 2))
                    steps.did(dve.tensor_tensor(TC[:, CPAD:CPAD + SEQ], TA[:, 0:SEQ], TB[:, 0:SEQ], ALU.mult))
                    steps.did(dve.tensor_tensor(own(TC)[:, :, CPAD:], by_row(TA[:, SEQ:TOK]),
                                                by_row(TB[:, SEQ:TOK]), ALU.mult))
                    steps.then(dve.tensor_copy(own(TC)[:, :, 0:CPAD], by_row(CSTATE[:, c, :])))
                    steps.did(dve.tensor_copy(CNEW[:, c, 0:CPAD], TC[:, SEQ:SEQ + CPAD]))
                    tap = lambda n: PAR[:, ds(c + (CONV_W + n * CH), 1)]
                    steps.then(dve.tensor_scalar(line(TD), line(TC, 2), tap(0), None, ALU.mult))
                    steps.then(dve.scalar_tensor_tensor(line(TD), line(TC, 1), tap(1), line(TD), ALU.mult, ALU.add))
                    steps.then(dve.scalar_tensor_tensor(line(TD), line(TC), tap(2), line(TD), ALU.mult, ALU.add))
                    dve.tensor_copy(by_row(CNEW[:, c, CPAD:]), own(TC)[:, :, DEC:]).then_inc(conv_kept, 1)
                    evacuate(2, TE)
                    dve.wait_ge(psum_free, i * 6 + (s0["tiles"] + 3 * j + 3))
                    dve.wait_ge(conv_kept, c + 1)
                    steps.then(dve.tensor_tensor(TB[:, 0:SEQ], TE[:, 0:SEQ], TD[:, CPAD:CPAD + SEQ], ALU.mult))
                    dve.tensor_tensor(by_row(TB[:, SEQ:TOK]), by_row(TE[:, SEQ:TOK]), own(TD)[:, :, CPAD:],
                                      ALU.mult).then_inc(values, 1)
                    dve.wait_ge(rounded, c + (s0["rounded"] + 1))
                    dve.tensor_tensor(B[:, c, 1, :], TB[:, 0:TOK], B[:, c, 0, :].bitcast(F32), ALU.subtract) \
                        .then_inc(b_ready, 1)
            down_last("conv_out", G_ATTN)

            rstd_tokens(2, START["q_proj"]["squares"])
            with dve.Fori(0, KT // 2) as i:
                for j in range(2):
                    convert_next(unit("q_proj", i, 2 * j))
                    product(unit("q_proj", i, 2 * j + 1))
                    dve.tensor_tensor(halves(Q[:, i * 2 + j, :]), M[:, 2 * j:2 * j + 2, 0:HALF],
                                      halves(RSTD[:, :]), ALU.mult).then_inc(psum_free, 1)
                    convert_next(unit("q_proj", i, 2 * j + 1))

            def attend(g):
                s = START[f"attend_{g}"]

                def negmax(e, n, scores):
                    steps.then(dve.tensor_reduce(ROWMAX[:, e:e + n], scores, AX.X, ALU.max))
                    dve.tensor_scalar(NEGMAX[:, e:e + n], ROWMAX[:, e:e + n], -SCALE, None, ALU.mult) \
                        .then_inc(negmax_ready, 1)

                def sample_max(j):
                    dve.wait_ge(cache_used, key_set(2 * g + j, SETS))
                    negmax(2 * j, 2, S[:, 2 + j, :].rearrange("p (r m) -> p r m", r=2))

                def prompt_max(p):
                    dve.wait_ge(heads_scored, 8 * g + p + 1)
                    negmax(4 + p, 1, M[:, p % 4, 0:MEM])

                def normalise(e):
                    dve.wait_ge(exps, 12 * g + e + 1)
                    steps.then(dve.reciprocal(ROWINV[:, e:e + 1], ROWSUM[:, e:e + 1]))
                    dve.tensor_scalar(PROBS[:, e, :], PROBS[:, e, :], ROWINV[:, e:e + 1], None, ALU.mult) \
                        .then_inc(probs_ready, 1)

                def copy_turned_samples(j):
                    item = TURNS * g + (0, 5)[j]
                    dve.wait_ge(turned, item + 1)
                    if g or j:
                        dve.wait_ge(cache_used, value_set(2 * g, SETS) if j else value_set(1, SETS))
                    dve.tensor_copy(PS[:, :, :, :].rearrange("p a r n -> p (a r n)"), S[:, turned_at(item), :]) \
                        .then_inc(turned_out, 1)

                def copy_turned(j, tt):
                    item = TURNS * g + (1, 7)[j] + tt
                    if (g or j) and tt == 0:
                        dve.wait_ge(pv_done, HT * (2 * g + j))
                    dve.wait_ge(turned, item + 1)
                    dve.tensor_copy(PT[:, :, tt * P:tt * P + P],
                                    S[:, turned_at(item), 0:2 * P].rearrange("p (a b) -> p a b", a=2)) \
                        .then_inc(turned_out, 1)

                def copy_samples_out(j, r):
                    dve.wait_ge(cache_used, value_set(2 * g + j, 2 * r + 2))
                    if g and not j:
                        dve.wait_ge(turned, TURNS)
                    dve.tensor_copy(OS[:, r, :], S[:, 2 + r, :]).then_inc(os_copied, 1)

                tiles = A if g == 0 else B

                def low_prompt(c):
                    dve.wait_ge(rounded, s["rounded"] + (1, 2, 3, 5, 6, 7, 8, 10)[c])
                    dve.tensor_tensor(tiles[:, c, 1, 0:SEQ], M[:, c % 4, 0:SEQ],
                                      tiles[:, c, 0, 0:SEQ].bitcast(F32), ALU.subtract).then_inc(b_ready, 1)

                def low_samples(j):
                    dve.wait_ge(rounded, s["rounded"] + (4, 9)[j])
                    head = slice(HT * j, HT * j + HT)
                    dve.tensor_tensor(tiles[:, head, 1, SEQ:TOK],
                                      S[:, turned_at(TURNS * g + (6, 11)[j]), 0:P]
                                      .rearrange("p (c n) -> p c n", c=HT),
                                      tiles[:, head, 0, SEQ:TOK].bitcast(F32), ALU.subtract) \
                        .then_inc(turned_out, 1)

                sample_max(0)
                sample_max(1)
                for e in (0, 1):
                    normalise(e)
                for p in range(4):
                    prompt_max(p)
                    normalise(2 + p)
                copy_turned_samples(0)
                prompt_max(4)
                normalise(6)
                prompt_max(5)
                normalise(7)
                copy_samples_out(0, 0)
                prompt_max(6)
                normalise(8)
                copy_turned(0, 0)
                prompt_max(7)
                normalise(9)
                copy_turned(0, 1)
                normalise(10)
                copy_turned(0, 2)
                normalise(11)
                copy_turned(0, 3)
                copy_samples_out(0, 1)
                low_prompt(0)
                copy_turned_samples(1)
                low_prompt(1)
                low_prompt(2)
                low_samples(0)
                copy_samples_out(1, 0)
                copy_turned(1, 0)
                copy_turned(1, 1)
                low_prompt(3)
                copy_turned(1, 2)
                copy_turned(1, 3)
                copy_samples_out(1, 1)
                low_prompt(4)
                low_prompt(5)
                low_prompt(6)
                low_samples(1)
                low_prompt(7)

            attend(0)
            down("o_proj_0")
            attend(1)
            down_last("o_proj_1", G_MLP)

            rstd_tokens(3, START["up_0"]["squares"])
            s0 = START["up_0"]

            def up(c):
                with dve.Fori(0, 4) as i:
                    for j in range(2):
                        n = c * 8 + i * 2
                        convert_next(unit("up_0", i + c * 8, 2 * j))
                        product(unit("up_0", i + c * 8, 2 * j + 1))
                        dve.wait_ge(values, n + (s0["values"] + j))
                        dve.scalar_tensor_tensor(halves(TA[:, 0:TOK]), M[:, 2 * j:2 * j + 2, 0:HALF], 0.0,
                                                 halves(RSTD[:, :]), ALU.max, ALU.mult).then_inc(psum_free, 1)
                        dve.wait_ge(psum_free, c * 24 + i * 2 + (s0["tiles"] + j + 1))
                        dve.wait_ge(b_ready, n + (s0["b"] + j))
                        dve.tensor_tensor(TB[:, 0:TOK], TA[:, 0:TOK], TA[:, 0:TOK], ALU.mult).then_inc(values, 1)
                        convert_next(unit("up_0", i + c * 8, 2 * j + 1))
                        dve.wait_ge(rounded, n + (s0["rounded"] + j + 1))
                        dve.tensor_tensor(B[:, i * 2 + j, 1, :], TB[:, 0:TOK], B[:, i * 2 + j, 0, :].bitcast(F32),
                                          ALU.subtract).then_inc(b_ready, 1)

            with dve.Fori(0, FF_CHUNKS - 1) as c:
                up(c)
                down("down_0", c * 8)
            up(FF_CHUNKS - 1)

            def final_tile(h, i, j, more=True):
                t, u, half = i * 4 + j, unit(f"final_{h}", i, j), slice(h * HALF, h * HALF + HALF)
                product(u)
                dve.tensor_tensor(X[:, t, half], M[:, j, 0:HALF], X[:, t, half], ALU.add).then_inc(psum_free, 1)
                if more:
                    convert_next(u)
                n = t + START[f"final_{h}"]["squares"]
                dve.wait_ge(squared, n + 1)
                dve.wait_ge(summed, n)
                dve.tensor_tensor(SUMS[:, half], SUMS[:, half], (TA, TB)[j % 2][:, 0:HALF], ALU.add) \
                    .then_inc(summed, 1)

            def final_rstd(h):
                half = slice(h * HALF, h * HALF + HALF)
                rstd(4 + h, S[:, h, 0:HALF], RSTD[:, half], RSTD[:, half])

            def output(h, t):
                half = slice(h * HALF, h * HALF + HALF)
                dve.scalar_tensor_tensor(Y[:, t, half], X[:, t, half], PAR[:, ds(t + G_FINAL, 1)], RSTD[:, half],
                                         ALU.mult, ALU.mult).then_inc(y_ready, 1)

            with dve.Fori(0, 4) as i:
                for j in range(4):
                    final_tile(0, i, j)
            for j in range(4):
                final_tile(1, 0, j)
            final_rstd(0)
            for t in range(4):
                output(0, t)
            with dve.Fori(1, 3) as i:
                for j in range(4):
                    final_tile(1, i, j)
                    output(0, i * 4 + j)
            for j in range(4):
                output(0, 12 + j)
                final_tile(1, 3, j, False)
            final_rstd(1)
            for t in range(KT):
                output(1, t)

        @block.tensor
        def _(pe):
            ones, ident = PAR[:, ONES:ONES + P], PAR[:, IDENT:IDENT + P]

            def split_products(outs, weights_at, inner, first, last):
                passes = [(WHI, 0), (WHI, 1), (WLO, 0)]
                for n, (w, part) in enumerate(passes):
                    for out, moving in zip(outs, inner(part)):
                        ins = pe.matmul(out, weights_at(w), moving, start=first and n == 0,
                                        stop=last and n == len(passes) - 1)
                return ins

            def multiply(u, m, tiles, k0, first, last, ready=None):
                pe.wait_ge(split_ready, count(u))
                outs = [M[:, 2 * m + h, 0:HALF] for h in range(2)]
                for kk in range(CH):
                    if ready:
                        ready(k0 + kk)
                    cols = slice(kk * P, kk * P + P)
                    ins = split_products(
                        outs, lambda w: w[:, u[1], cols],
                        lambda part: [tiles[:, k0 + kk, part, h * HALF:h * HALF + HALF] for h in range(2)],
                        first and kk == 0, last and kk == CH - 1)
                ins.then_inc(units_used, 1)

            def up_tile(name, extra, n, t, ready=None, between=None):
                pe.wait_ge(psum_free, t + (-1))
                m = n // 2 % 2
                multiply(unit(name, extra, n), m, A, 0, True, False, ready)
                if between:
                    between()
                multiply(unit(name, extra, n + 1), m, A, CH, False, True, ready)

            def up(name, tiles, extra=0, t0=None, first=0):
                t0 = START[name]["tiles"] if t0 is None else t0
                with pe.Fori(first, tiles // 2) as i:
                    for j in range(2):
                        up_tile(name, i + extra, 2 * j, i * 2 + j + t0)

            def down(name, tiles, ready, extra=0, t0=None, apart=False):
                t0 = START[name]["tiles"] if t0 is None else t0

                def group(i, js):
                    for j in js:
                        pe.wait_ge(psum_free, i * 4 + t0 + (j - 1))
                        multiply(unit(name, i + extra, j), j % 2, tiles, 0, True, True, ready if j == 0 else None)

                if apart:
                    for j in range(2):
                        multiply(unit(name, extra, j), j, tiles, 0, True, True, ready if j == 0 else None)
                    group(0, (2, 3))
                with pe.Fori(1 if apart else 0, 4) as i:
                    group(i, range(4))

            def sum_squares(n, squares, halves=(0, 1)):
                pe.wait_ge(summed, squares)
                for h in halves:
                    ins = pe.matmul(S[:, h, 0:HALF], ones, SUMS[:, h * HALF:h * HALF + HALF], start=True, stop=True)
                ins.then_inc(sums_done, 1)

            def ready_by(semaphore, counts):
                return lambda k: pe.wait_ge(semaphore, counts(k))

            pe.wait_ge(par_loaded, 16)

            def key_tile(i, j, peeled, between=None):
                if not peeled:
                    pe.wait_ge(psum_free, i * 4 + (j - 3))
                for half in range(2):
                    u = unit("k_proj", i * 2, 2 * j + half)
                    pe.wait_ge(split_ready, count(u))
                    for kk in range(CH):
                        k = CH * half + kk
                        if peeled and j == 0:
                            pe.wait_ge(mem_ready, k + 1)
                        ins = split_products([M[:, j, 0:MEM]], lambda w: w[:, u[1], kk * P:kk * P + P],
                                             lambda part: [MEMS[:, k, part, :]], k == 0, k == KT - 1)
                    ins.then_inc(units_used, 1)
                    if half == 1 and between:
                        between()

            def sum_memory():
                pe.wait_ge(summed, CH)
                for a in range(2):
                    pe.matmul(S[:, 0, 0:MEM], ones, TE[:, a * MEM:a * MEM + MEM], start=a == 0, stop=a == 1)
                for j in range(2):
                    for a in range(2):
                        col = a * MEM + j * P
                        ins = pe.matmul(S[:, 0, MEM + j:MEM + j + 1], TE[:, col:col + P], ones[:, 0:1],
                                        start=a == 0, stop=a == 1)
                ins.then_inc(sums_done, 1)

            for j in range(4):
                key_tile(0, j, True, sum_memory if j == 2 else None)
            with pe.Fori(1, KT // 4) as i:
                for j in range(4):
                    key_tile(i, j, False)

            def value_tile(extra, i):
                for n in range(8):
                    u = unit("v_proj", extra, 8 * i + n)
                    pe.wait_ge(split_ready, count(u))
                    for kk in range(2):
                        for mt in range(2):
                            for x, (part, w) in enumerate(((0, WHI), (0, WLO), (1, WHI))):
                                ins = pe.matmul(M[:, 2 * i + mt, 0:512],
                                                MEMS[:, 2 * n + kk, part, mt * P:mt * P + P],
                                                w[:, u[1], kk * 512:kk * 512 + 512],
                                                start=(n + kk + x == 0), stop=(n == 7 and kk == 1 and x == 2))
                    ins.then_inc(units_used, 1)

            for i in range(2):
                pe.wait_ge(psum_free, KT - 2 + 2 * i)
                value_tile(0, i)
            for i in range(2):
                pe.wait_ge(v_staged, 2 * i + 2)
                value_tile(4, i)

            sum_squares(1, START["pool_in"]["squares"])
            pe.wait_ge(a_ready, KT)
            for j in range(2):
                pe.wait_ge(v_staged, 6 + 2 * j)
                up_tile("pool_in", 0, 2 * j, START["pool_in"]["tiles"] + j)
            up("pool_in", CH, first=1)

            s0 = START["pool_map"]
            pe.wait_ge(var_ready, 2)
            for c in range(CH):
                g, n = c // 2, c % 2
                u = unit("pool_map", 0, g // 2)
                if c % 4 == 0:
                    pe.wait_ge(split_ready, count(u))
                if c < 2:
                    pe.wait_ge(psum_free, s0["tiles"] - 1 + c)
                else:
                    pe.wait_ge(psum_free, s0["tiles"] + max(0, c - 3))
                out = pool_map_out(c)
                for kk in range(2):
                    pe.wait_ge(b_ready, 2 * g + kk + 1)
                    col = ((g % 2 * 2 + kk) * 2 + n) * P
                    ins = split_products(
                        [out[:, h, :] for h in range(2)], lambda w: w[:, u[1], col:col + P],
                        lambda part: [B[:, 2 * g + kk, part, h * HALF:h * HALF + HALF] for h in range(2)],
                        kk == 0, kk == 1)
                if n == 1:
                    ins.then_inc(units_used if g % 2 else group_done, 1)

            down("pool_out", B, ready_by(psum_free, lambda k: s0["tiles"] + max(5, k + 1)), apart=True)
            s1 = START["conv_in"]
            with pe.Fori(0, CH // 2) as i:
                for n in range(6):
                    up_tile("conv_in", i * 3, 2 * n, i * 6 + (n + s1["tiles"]))
            down("conv_out", B, ready_by(b_ready, lambda k: s1["b"] + k + 1))

            def first_pair(name, n, squares, a0):
                t0 = START[name]["tiles"]
                up_tile(name, 0, 0, t0, ready_by(a_ready, lambda k: a0 + k + 1))
                sum_squares(n, squares)
                up_tile(name, 0, 2, t0 + 1)

            first_pair("q_proj", 2, START["q_proj"]["squares"], KT)

            def keys_of_caches(h, n):
                at, r = key_set(h, n), n // 2
                pe.wait_ge(cache_loaded[at % 2], 16 * (at // 2 + 1))
                for kk in range(2):
                    k = n % 2 * 2 + kk
                    for j in range(GROUPS):
                        ins = pe.matmul(S[32 * j:32 * j + 32, 2 + h % 2, r * MEM:r * MEM + MEM],
                                        Q[:, HT * h + k, SEQ:TOK], cache_ring(at)[:, j, kk * MEM:kk * MEM + MEM],
                                        start=k == 0, stop=k == HT - 1)
                ins.then_inc(cache_used, 1)

            def query_pair(i):
                for j in range(2):
                    up_tile("q_proj", i, 2 * j, i * 2 + j + START["q_proj"]["tiles"])

            for i in range(1, 6):
                query_pair(i)
                if i >= 2:
                    for n in (2 * i - 4, 2 * i - 3):
                        h = n // SETS
                        pe.wait_ge(psum_free, START["q_proj"]["tiles"] + HT * (h + 1))
                        keys_of_caches(h, n % SETS)
            up("q_proj", KT, first=6)

            def attend(g):
                s = START[f"attend_{g}"]

                def prompt_scores(p):
                    j, tt = p // 4, p % 4
                    h = 2 * g + j
                    if tt == 0:
                        pe.wait_ge(keys_loaded[j], 16 * (g + 1))
                    if p >= 4:
                        pe.wait_ge(exps, 12 * g + p + 1)
                    elif p % 2 == 0:
                        pe.wait_ge(psum_free, s["tiles"] - 1 + p // 2)
                    for dk in range(HT):
                        keys = KV[:, 1, dk * MEM:dk * MEM + MEM] if j else KEYS[:, dk * MEM:dk * MEM + MEM]
                        ins = pe.matmul(M[:, p % 4, 0:MEM], Q[:, HT * h + dk, tt * P:tt * P + P], keys,
                                        start=dk == 0, stop=dk == HT - 1)
                    ins.then_inc(heads_scored, 1)

                def turn_bank(item):
                    item += TURNS * g
                    if item >= 2:
                        pe.wait_ge(turned_out, item - 1)
                    return S[:, turned_at(item), :]

                def turn_sample_probs(j):
                    pe.wait_ge(probs_ready, 12 * g + 2 * j + 2)
                    out = turn_bank((0, 5)[j])
                    for mt in range(2):
                        for r in range(2):
                            col = (2 * mt + r) * P
                            ins = pe.transpose(out[:, col:col + P], PROBS[:, 2 * j + r, mt * P:mt * P + P], ident)
                    ins.then_inc(turned, 1)

                def turn_probs(j, tt):
                    e = 4 + 4 * j + tt
                    pe.wait_ge(probs_ready, 12 * g + e + 1)
                    out = turn_bank((1, 7)[j] + tt)
                    for mt in range(2):
                        ins = pe.transpose(out[:, mt * P:mt * P + P], PROBS[:, e, mt * P:mt * P + P], ident)
                    ins.then_inc(turned, 1)

                def values_of_caches(j, n):
                    at, r, mt = value_set(2 * g + j, n), n // 2, n % 2
                    if mt == 0:
                        if j:
                            pe.wait_ge(os_copied, 4 * g + r + 1)
                        else:
                            pe.wait_ge(exps, 12 * g + 2 * r + 2)
                        pe.wait_ge(turned_out, TURNS * g + (1, 6)[j])
                    pe.wait_ge(cache_loaded[at % 2], 16 * (at // 2 + 1))
                    for i in range(GROUPS):
                        ins = pe.matmul(S[32 * i:32 * i + 32, 2 + r, :], PS[:, mt, r, 32 * i:32 * i + 32],
                                        cache_ring(at)[:, i, :], start=mt == 0, stop=mt == 1)
                    ins.then_inc(cache_used, 1)

                def turn_samples_out(j):
                    pe.wait_ge(os_copied, 4 * g + 2 * j + 2)
                    out = turn_bank((6, 11)[j])
                    for m in range(HT):
                        for r in range(2):
                            own = OWN + r * SAMPLE
                            ins = pe.matmul(out[:, m * SAMPLE:m * SAMPLE + SAMPLE], OS[:, r, m * P:m * P + P],
                                            PAR[:, own:own + SAMPLE], start=r == 0, stop=r == 1)
                    ins.then_inc(turned, 1)

                def prompt_out(c):
                    j, n = c // HT, c % HT
                    if n == 0:
                        pe.wait_ge(values_loaded[j], 16 * (g + 1))
                        pe.wait_ge(turned_out, TURNS * g + (5, 11)[j])
                    if j:
                        pe.wait_ge(b_ready, s["b"] + n + 1)
                    elif n == 0:
                        pe.wait_ge(exps, 12 * g + 12)
                    for mt in range(2):
                        col = mt * HD + n * P
                        ins = pe.matmul(M[:, c % 4, 0:SEQ], KV[:, j, col:col + P], PT[:, mt, :],
                                        start=mt == 0, stop=mt == 1)
                    ins.then_inc(pv_done, 1)

                for p in range(4):
                    prompt_scores(p)
                turn_sample_probs(0)
                prompt_scores(4)
                prompt_scores(5)
                values_of_caches(0, 0)
                values_of_caches(0, 1)
                prompt_scores(6)
                turn_probs(0, 0)
                prompt_scores(7)
                turn_probs(0, 1)
                values_of_caches(0, 2)
                turn_probs(0, 2)
                turn_probs(0, 3)
                values_of_caches(0, 3)
                prompt_out(0)
                turn_sample_probs(1)
                prompt_out(1)
                values_of_caches(1, 0)
                prompt_out(2)
                turn_samples_out(0)
                values_of_caches(1, 1)
                turn_probs(1, 0)
                turn_probs(1, 1)
                prompt_out(3)
                values_of_caches(1, 2)
                turn_probs(1, 2)
                turn_probs(1, 3)
                values_of_caches(1, 3)
                prompt_out(4)
                prompt_out(5)
                prompt_out(6)
                turn_samples_out(1)
                prompt_out(7)

            def attended(g):
                def wait(k):
                    pe.wait_ge(b_ready, START[f"attend_{g}"]["b"] + max(6, k + 1))
                    if k in (0, HT):
                        pe.wait_ge(turned_out, TURNS * g + (12 if k else 7))
                return wait

            attend(0)
            for i in range(4):
                for j in range(4):
                    t = i * 4 + j
                    if t:
                        pe.wait_ge(psum_free, START["o_proj_0"]["tiles"] + t - 1)
                    multiply(unit("o_proj_0", i, j), j % 2, A, 0, True, True, attended(0) if t == 0 else None)
                for n in (2 * i, 2 * i + 1):
                    keys_of_caches(2 + n // SETS, n % SETS)
            attend(1)
            down("o_proj_1", B, attended(1))

            s2 = START["up_0"]
            first_pair("up_0", 3, s2["squares"], 2 * KT)
            up("up_0", CH, first=1)
            down("down_0", B, ready_by(b_ready, lambda k: s2["b"] + k + 1))
            with pe.Fori(1, FF_CHUNKS - 1) as c:
                up("up_0", CH, c * 8, c * 24 + s2["tiles"])
                down("down_0", B, ready_by(b_ready, lambda k: c * 8 + (s2["b"] + k + 1)), c * 8,
                     c * 24 + START["down_0"]["tiles"])
            last = f"up_{FF_CHUNKS - 1}"
            up(last, CH)

            def final_tile(h, i, j):
                u = unit(f"final_{h}", i, j)
                pe.wait_ge(psum_free, i * 4 + (START[f"final_{h}"]["tiles"] + j - 3))
                pe.wait_ge(split_ready, count(u))
                for k in range(CH):
                    if h == 0 and j == 0:
                        pe.wait_ge(b_ready, START[last]["b"] + k + 1)
                    ins = split_products([M[:, j, 0:HALF]], lambda w: w[:, u[1], k * P:k * P + P],
                                         lambda part: [B[:, k, part, h * HALF:h * HALF + HALF]],
                                         k == 0, k == CH - 1)
                ins.then_inc(units_used, 1)

            pe.wait_ge(psum_free, START["final_0"]["tiles"] - 1)
            with pe.Fori(0, 4) as i:
                for j in range(4):
                    final_tile(0, i, j)
            for j in range(4):
                final_tile(1, 0, j)
                if j == 2:
                    sum_squares(4, START["final_1"]["squares"], (0,))
            with pe.Fori(1, 4) as i:
                for j in range(4):
                    final_tile(1, i, j)
            sum_squares(5, TOTAL["squares"], (1,))


def layout(np, inputs):
    a = {k: np.asarray(v) for k, v in inputs.items()}

    def over_all(w):
        n = w.shape[1] // P
        return w.reshape(2, CH, P, n, P).transpose(3, 0, 2, 1, 4).reshape(2 * n, P, UNIT)

    def over_half(w):
        return w.reshape(CH, P, KT, P).transpose(2, 1, 0, 3).reshape(KT, P, UNIT)

    w_in, w_out, w_o = a["w_in"][0], a["w_out"][0], a["w_o"][0]
    w_up, w_down = a["w_up"][0], a["w_down"][0]
    half = CH * P

    def turned(v):
        return v.reshape(4, -1, *v.shape[1:])[::-1].reshape(v.shape)

    conv = over_all(w_in[:, half:]).reshape(3, CH, 2, P, UNIT)
    conv = conv[[1, 2, 0]].transpose(1, 0, 2, 3, 4).reshape(6 * CH, P, UNIT)
    units = [
        over_all(a["w_k"][0]),
        a["w_v"][0].reshape(8, 2, P, 4, 512).transpose(3, 0, 2, 1, 4).reshape(32, P, UNIT),
        over_all(turned(w_in[:, :half].T).T),
        a["w_pool"][0][::-1].reshape(2, 2, 2, P, 2 * P).transpose(0, 3, 1, 2, 4).reshape(2, P, UNIT),
        over_half(turned(w_out[:half])), conv, over_half(w_out[half:]),
        over_all(a["w_q"][0]), over_half(w_o[:half]), over_half(w_o[half:])]
    for c in range(FF_CHUNKS):
        units += [over_all(w_up[:, c * half:c * half + half]), over_half(w_down[c * half:c * half + half])]
    units.append(units[-1])
    weights = np.concatenate(units)
    assert weights.shape[0] == UNITS

    def column(v):
        return v.reshape(-1, P).T

    inv = np.broadcast_to((1.0 / np.arange(1, PAD + 1)).astype(np.float32), (P, PAD))
    own = np.zeros((GROUPS, NB, DEC, 2, NB, DEC), np.float32)
    for b in range(NB):
        for t in range(DEC):
            own[b // 2, b, t, b % 2, b, t] = 1
    params = np.concatenate(
        [column(a["norm_mix"][0]), column(a["norm_attn"][0]), column(a["norm_mem"][0]), column(a["norm_mlp"][0]),
         column(a["norm_final"]), column(turned(a["pool_scale"][0])), column(a["conv_w"][0].reshape(-1)),
         np.ones((P, P), np.float32), np.eye(P, dtype=np.float32), inv,
         own.reshape(P, 2 * SAMPLE)], axis=1)
    x_t = np.concatenate([a["x_prompt"][0], a["x_sample"].reshape(SAMPLE, D)]).T
    pool_state = np.zeros((CH, P, NB, PAD), np.float32)
    pool_state[:, :, :, 1:] = turned(a["state_pool"][0].transpose(2, 0, 1)).reshape(CH, P, NB, POOL_KEEP)
    arrays = {
        "weights": weights, "x_t": x_t, "mem_t": a["mem_prompt"][0].T, "params": params,
        "cache_k": a["cache_mem_k"][0].reshape(GROUPS, 2, MEM, HEADS, 2, 2, P).transpose(3, 1, 4, 6, 0, 5, 2)
        .reshape(HEADS * SETS, P, GROUPS * 512),
        "cache_v": a["cache_mem_v"][0].reshape(GROUPS, 2, 2, P, HEADS, HD).transpose(4, 1, 2, 3, 0, 5)
        .reshape(HEADS * SETS, P, GROUPS * 512),
        "pool_state": pool_state.reshape(CH, P, NB * PAD),
        "conv_state": a["state_conv"][0].transpose(2, 0, 1).reshape(CH, P, NB * CPAD).transpose(1, 0, 2),
    }
    return {k: np.ascontiguousarray(v) for k, v in arrays.items()}


def kernel(**inputs):
    import numpy as np
    import concourse.bacc as bacc
    from concourse.bass_utils import run_bass_kernel_spmd

    nc = bacc.Bacc("TRN2", target_bir_lowering=False, num_devices=1)
    arrays = layout(np, inputs)
    args = [nc.dram_tensor(name, a.shape, F32, kind="ExternalInput").ap() for name, a in arrays.items()]
    outs = {"y_t": (2, P, KT, HALF), "k_t": (KT, P, MEM), "v_out": (4, 2, P, 512),
            "pool_new": (CH, P, (NB + 1) * POOL_KEEP), "conv_new": (P, CH, (NB + 1) * CPAD)}
    args += [nc.dram_tensor(name, shape, F32, kind="ExternalOutput").ap() for name, shape in outs.items()]
    build(nc, *args)
    r = run_bass_kernel_spmd(nc, [arrays], core_ids=[0]).results[0]
    y_t, k_t, v_out, pool_new, conv_new = (np.asarray(r[name]) for name in outs)

    y = y_t.transpose(0, 3, 2, 1).reshape(TOK, D)
    keys = k_t.reshape(D, MEM).T.reshape(1, 1, MEM, HEADS, HD)
    vals = v_out.reshape(4, MEM, 512).transpose(1, 0, 2).reshape(1, 1, MEM, HEADS, HD)
    pools = pool_new.reshape(4, -1)[::-1].reshape(CH * P, NB + 1, POOL_KEEP).transpose(1, 2, 0)
    convs = conv_new.transpose(1, 0, 2).reshape(CH * P, NB + 1, CPAD).transpose(1, 2, 0)
    out = (y[:SEQ].reshape(1, SEQ, D), y[SEQ:].reshape(NB, DEC, D), pools[None, :1], convs[None, :1], keys, vals,
           pools[None, 1:], convs[None, 1:])
    return tuple(np.ascontiguousarray(x) for x in out)
```
